# Optimizing a Trainium2 kernel written in Bass

```python
import math
import jax, jax.numpy as jnp
from jax import lax
import numpy as np

D_MODEL = 2048
BATCH = 1
SEQ = 512
DEPTH = 2

D_INNER_A = D_MODEL
SSD_HEAD_DIM = 64
SSD_HEADS = D_INNER_A // SSD_HEAD_DIM
SSD_GROUPS = 4
SSD_STATE = 128
SSD_CHUNK = 128
CONV_WIDTH = 4
CONV_DIM = D_INNER_A + 2 * SSD_GROUPS * SSD_STATE
D_INNER_B = D_MODEL
SGU_CHUNK = 128
SGU_GROUP_DIM = 128
SGU_GROUPS = D_INNER_B // SGU_GROUP_DIM
D_INNER_C = D_MODEL
SB_HEAD_DIM = 128
SB_HEADS = D_INNER_C // SB_HEAD_DIM
SB_BLOCK = 128
EVEN_IN = 2 * D_INNER_A + 2 * SSD_GROUPS * SSD_STATE + SSD_HEADS + 3 * D_INNER_B
ODD_IN = 4 * D_INNER_C
N_EVEN = (DEPTH + 1) // 2
N_ODD = DEPTH // 2
NORM_EPS = 1e-5

kernel_name = "hybrid_ssd_sgu_stickbreak_trunk"

def rms_norm(x, w, eps=NORM_EPS):
    xf = x.astype(jnp.float32)
    xf = xf * lax.rsqrt(jnp.mean(xf * xf, axis=-1, keepdims=True) + eps)
    return xf.astype(x.dtype) * w

def layer_norm(x, w, b, eps=NORM_EPS):
    xf = x.astype(jnp.float32)
    mu = jnp.mean(xf, axis=-1, keepdims=True)
    xc = xf - mu
    xf = xc * lax.rsqrt(jnp.mean(xc * xc, axis=-1, keepdims=True) + eps)
    return xf.astype(x.dtype) * w + b

def causal_depthwise_conv(x, w, b):
    c = x.shape[-1]
    k = w.shape[0]
    y = lax.conv_general_dilated(
        x, w[:, None, :], window_strides=(1,), padding=((k - 1, 0),),
        dimension_numbers=("NWC", "WIO", "NWC"), feature_group_count=c)
    return y + b

def ssd_scan(xs, dt, b_in, c_in, a_log, d_skip):
    bsz, s, _ = xs.shape
    nc, L = s // SSD_CHUNK, SSD_CHUNK
    G, R, P, N = SSD_GROUPS, SSD_HEADS // SSD_GROUPS, SSD_HEAD_DIM, SSD_STATE
    f32 = jnp.float32
    a = -jnp.exp(a_log.astype(f32))
    x_h = xs.reshape(bsz, s, SSD_HEADS, P).astype(f32)
    x_c = (x_h * dt[..., None]).reshape(bsz, nc, L, G, R, P)
    b_c = b_in.astype(f32).reshape(bsz, nc, L, G, N)
    c_c = c_in.astype(f32).reshape(bsz, nc, L, G, N)
    a_dt = (dt * a).reshape(bsz, nc, L, G, R)
    cs = jnp.cumsum(a_dt, axis=2)
    causal = jnp.tril(jnp.ones((L, L), dtype=bool))[None, None, :, :, None, None]
    seg = cs[:, :, :, None] - cs[:, :, None, :]
    decay = jnp.exp(jnp.where(causal, seg, -jnp.inf))
    scores = jnp.einsum("bclgn,bcsgn->bclsg", c_c, b_c)
    y_diag = jnp.einsum("bclsg,bclsgr,bcsgrp->bclgrp", scores, decay, x_c)
    end_decay = jnp.exp(cs[:, :, -1:] - cs)
    states = jnp.einsum("bclgn,bclgr,bclgrp->bcgrpn", b_c, end_decay, x_c)
    chunk_decay = jnp.exp(cs[:, :, -1])

    def step(h, inp):
        st, dec = inp
        return dec[..., None, None] * h + st, h

    h0 = jnp.zeros((bsz, G, R, P, N), f32)
    _, prev = lax.scan(step, h0, (jnp.moveaxis(states, 1, 0), jnp.moveaxis(chunk_decay, 1, 0)))
    prev = jnp.moveaxis(prev, 0, 1)
    y_off = jnp.einsum("bclgn,bcgrpn,bclgr->bclgrp", c_c, prev, jnp.exp(cs))
    y = (y_diag + y_off).reshape(bsz, s, SSD_HEADS, P) + x_h * d_skip.astype(f32)[:, None]
    return y.reshape(bsz, s, D_INNER_A).astype(xs.dtype)

def chunked_sgu(u, v, ln_w, ln_b, w_s, b_s):
    bsz, s, _ = u.shape
    nc = s // SGU_CHUNK
    u = jax.nn.gelu(u)
    v = layer_norm(jax.nn.gelu(v), ln_w, ln_b)
    v_c = v.reshape(bsz, nc, SGU_CHUNK, SGU_GROUPS, SGU_GROUP_DIM)
    w_causal = jnp.tril(w_s)
    mixed = jnp.einsum("gts,bcsgd->bctgd", w_causal, v_c) + b_s.T[:, :, None]
    return u * mixed.reshape(bsz, s, D_INNER_B)

def stick_breaking_attention(q, k, v):
    bsz, s, _, d = q.shape
    scale = d ** -0.5
    outs = []
    for blk in range(s // SB_BLOCK):
        q0, q1 = blk * SB_BLOCK, (blk + 1) * SB_BLOCK
        qb = q[:, q0:q1].astype(jnp.float32)
        kb = k[:, :q1].astype(jnp.float32)
        z = jnp.einsum("bthd,bshd->bhts", qb, kb) * scale
        mask = jnp.arange(q1)[None, :] < jnp.arange(q0, q1)[:, None]
        log_keep = jnp.where(mask, -jax.nn.softplus(z), 0.0)
        after = lax.cumsum(log_keep, axis=3, reverse=True) - log_keep
        w = jnp.where(mask, jnp.exp(jax.nn.log_sigmoid(z) + after), 0.0)
        outs.append(jnp.einsum("bhts,bshd->bthd", w.astype(v.dtype), v[:, :q1]))
    return jnp.concatenate(outs, axis=1)

def even_layer(h, w_in, conv_w, conv_b, dt_bias, a_log, d_skip, ssd_norm_w,
               sgu_ln_w, sgu_ln_b, sgu_w, sgu_b, w_out):
    proj = h @ w_in
    o1 = D_INNER_A
    o2 = o1 + CONV_DIM
    o3 = o2 + SSD_HEADS
    o4 = o3 + D_INNER_B
    o5 = o4 + D_INNER_B
    z_a, xbc, dt_raw, g_b, u_b, v_b = jnp.split(proj, [o1, o2, o3, o4, o5], axis=-1)
    xbc = jax.nn.silu(causal_depthwise_conv(xbc, conv_w, conv_b))
    xs, b_in, c_in = jnp.split(xbc, [D_INNER_A, D_INNER_A + SSD_GROUPS * SSD_STATE], axis=-1)
    dt = jax.nn.softplus(dt_raw.astype(jnp.float32) + dt_bias.astype(jnp.float32))
    y_a = ssd_scan(xs, dt, b_in, c_in, a_log, d_skip)
    y_a = rms_norm(y_a * jax.nn.silu(z_a), ssd_norm_w)
    y_b = chunked_sgu(u_b, v_b, sgu_ln_w, sgu_ln_b, sgu_w, sgu_b) * jax.nn.silu(g_b)
    return jnp.concatenate([y_a, y_b], axis=-1) @ w_out

def odd_layer(h, w_in, w_out):
    bsz, s, _ = h.shape
    q, k, v, g = jnp.split(h @ w_in, 4, axis=-1)
    shp = (bsz, s, SB_HEADS, SB_HEAD_DIM)
    y = stick_breaking_attention(q.reshape(shp), k.reshape(shp), v.reshape(shp))
    return (y.reshape(bsz, s, D_INNER_C) * jax.nn.silu(g)) @ w_out

def setup_inputs(seed: int = 0) -> dict:
    key = jax.random.key(seed)
    ks = jax.random.split(key, 20)
    f32 = jnp.float32
    nrm = lambda k, shp, sc: jax.random.normal(k, shp, f32) * sc
    dt = jnp.exp(jax.random.uniform(ks[5], (N_EVEN, SSD_HEADS), f32)
                 * (math.log(0.1) - math.log(0.001)) + math.log(0.001))
    return {
        "x": jax.random.normal(ks[0], (BATCH, SEQ, D_MODEL), f32),
        "norm_w": 1.0 + nrm(ks[1], (DEPTH, D_MODEL), 0.05),
        "final_norm_w": 1.0 + nrm(ks[2], (D_MODEL,), 0.05),
        "ev_w_in": nrm(ks[3], (N_EVEN, D_MODEL, EVEN_IN), D_MODEL ** -0.5),
        "ev_conv_w": nrm(ks[4], (N_EVEN, CONV_WIDTH, CONV_DIM), CONV_WIDTH ** -0.5),
        "ev_conv_b": nrm(ks[6], (N_EVEN, CONV_DIM), 0.02),
        "ev_dt_bias": dt + jnp.log(-jnp.expm1(-dt)),
        "ev_a_log": jnp.log(jax.random.uniform(ks[7], (N_EVEN, SSD_HEADS), f32, 1.0, 16.0)),
        "ev_d_skip": 1.0 + nrm(ks[8], (N_EVEN, SSD_HEADS), 0.1),
        "ev_ssd_norm_w": 1.0 + nrm(ks[9], (N_EVEN, D_INNER_A), 0.05),
        "ev_sgu_ln_w": 1.0 + nrm(ks[10], (N_EVEN, D_INNER_B), 0.05),
        "ev_sgu_ln_b": nrm(ks[11], (N_EVEN, D_INNER_B), 0.02),
        "ev_sgu_w": nrm(ks[12], (N_EVEN, SGU_GROUPS, SGU_CHUNK, SGU_CHUNK), SGU_CHUNK ** -0.5),
        "ev_sgu_b": 1.0 + nrm(ks[13], (N_EVEN, SGU_GROUPS, SGU_CHUNK), 0.1),
        "ev_w_out": nrm(ks[14], (N_EVEN, D_INNER_A + D_INNER_B, D_MODEL), (D_INNER_A + D_INNER_B) ** -0.5),
        "od_w_in": nrm(ks[15], (N_ODD, D_MODEL, ODD_IN), D_MODEL ** -0.5),
        "od_w_out": nrm(ks[16], (N_ODD, D_INNER_C, D_MODEL), D_INNER_C ** -0.5),
    }

def reference(x, norm_w, final_norm_w, ev_w_in, ev_conv_w, ev_conv_b, ev_dt_bias,
              ev_a_log, ev_d_skip, ev_ssd_norm_w, ev_sgu_ln_w, ev_sgu_ln_b,
              ev_sgu_w, ev_sgu_b, ev_w_out, od_w_in, od_w_out):
    h = x
    for layer in range(DEPTH):
        hn = rms_norm(h, norm_w[layer])
        i = layer // 2
        if layer % 2 == 0:
            delta = even_layer(hn, ev_w_in[i], ev_conv_w[i], ev_conv_b[i], ev_dt_bias[i],
                               ev_a_log[i], ev_d_skip[i], ev_ssd_norm_w[i], ev_sgu_ln_w[i],
                               ev_sgu_ln_b[i], ev_sgu_w[i], ev_sgu_b[i], ev_w_out[i])
        else:
            delta = odd_layer(hn, od_w_in[i], od_w_out[i])
        h = h + delta
    return rms_norm(h, final_norm_w)


_drawn_inputs = setup_inputs


def setup_inputs(seed=0):
    import zlib

    import numpy as np

    out = dict(_drawn_inputs(seed))
    spreads = {}
    factors = {'ev_conv_b': 3.199,
     'ev_sgu_ln_w': 7.038,
     'ev_sgu_ln_b': 27.805,
     'ev_ssd_norm_w': 2.742,
     'ev_sgu_b': 3.382}
    for name, (base, spread) in spreads.items():
        noise = np.random.default_rng([zlib.crc32(name.encode()), seed]).standard_normal(out[name].shape)
        drawn = base * np.exp(spread * noise) if base else spread * noise
        out[name] = __import__('jax').numpy.asarray(drawn.astype(out[name].dtype))
    for name, factor in factors.items():
        out[name] = (out[name] * factor).astype(out[name].dtype)
    return out
```

```python
from contextlib import ExitStack

import numpy as np

import concourse.bass as bass
from concourse import mybir

P = 128
D = 2048
T = 512
KT = D // P
HK = KT // 2
NCH = T // P
HEADS_A, PD, GROUPS = 32, 64, 4
RH = HEADS_A // GROUPS
HEADS_C = 16
EPS = 1e-5
NCONV = 24
T_DT, T_B, T_C, T_X, T_Z, T_V, T_UG, T_OB, T_OA, T_AT, T_OO, T_END = (
    0, 1, 5, 9, 25, 41, 57, 89, 105, 121, 185, 201)
OUT_BY_POOL = (2, 5, 8, 11, 14)
X_PARTS = ((0, 1), (1, 4), (4, 8), (8, 12), (12, 16))
RING = 4
C_NW0, C_NW1, C_FNW, C_SSDW, C_CW, C_CB, C_D, C_DTB, C_ALOG, C_END = (
    0, 16, 32, 48, 64, 160, 184, 216, 217, 218)


def trunk(nc, xT, weights, table, shapes, sgu_wT, sgu_rows, out):
    F32, F32R = mybir.dt.float32, mybir.dt.float32r
    ALU, ACT = mybir.AluOpType, mybir.ActivationFunctionType
    ds = bass.ds

    z_dram = nc.dram_tensor("z_gate", (KT, P, T), F32, kind="Internal").ap()
    ya_dram = nc.dram_tensor("y_ssd", (KT, P, T), F32, kind="Internal").ap()
    v_dram = nc.dram_tensor("v_token_major", (KT, P, T), F32, kind="Internal").ap()
    cs_dram = nc.dram_tensor("cum_decay", (HEADS_A + RH, T), F32, kind="Internal").ap()

    ctx = ExitStack()
    with ctx:
        def sb(name, shape, dt=F32):
            return ctx.enter_context(nc.sbuf_tensor(name, shape, dt))

        def bank(name):
            return ctx.enter_context(nc.psum_tensor(name, [P, T], F32))

        def sem(name):
            return ctx.enter_context(nc.semaphore(name))

        w_raw = sb("w_raw", [P, RING, HK * P])
        w_hi = sb("w_hi", [P, RING, HK * P], F32R)
        w_lo = sb("w_lo", [P, RING, HK * P], F32R)
        a_hi = sb("a_hi", [P, KT, T], F32R)
        a_lo = sb("a_lo", [P, KT, T], F32R)
        big = sb("big", [P, KT, T])
        res = sb("res", [P, KT, T])
        work = sb("work", [P, 7900])

        def part(off, n):
            return work[:, off:off + n]

        ident, ones, causal, strict, negmask = (part(P * n, P) for n in range(5))
        tab = part(5 * P, C_END)
        tok = part(860, 384).rearrange("p (q c h) -> p q c h", q=3, c=NCH)
        rstd = part(1244, T)
        ssum = part(1756, T)
        S0 = 2268

        def ws(off, n=T):
            return part(S0 + off, n)

        zeros = ws(2048)
        var_t, root_t, newt_t = ws(4096), ws(4608), ws(5120)
        cv = [ws(0), ws(512)]
        xs = [ws(1024), ws(1536)]
        dec = ws(0, RH * P)
        ecs = ws(1024, RH * P)
        x_st, xw, ysq = ws(2048), ws(2560), ws(3072)
        state = ws(3584)
        zya = ws(4096)
        smask = ws(4608, P)
        b_st, bt_st = ws(4736, P), ws(4864, P)
        vcv = ws(4992)
        csb = res[:, 12:14, :].rearrange("p a t -> p (a t)")
        stats = res[:, 14, 0:NCH * KT * 6].rearrange("p (c k s) -> p c k s", c=NCH, k=KT)

        def stats_flat(c, k):
            return res[:, 14, ds(k * 6 + c * KT * 6, 6)]

        end_decay = res[:, 14, 400:400 + RH]
        mv = res[:, 14, 384:392].rearrange("p (c s) -> p c s", c=NCH)
        vrs = res[:, 14, 392:400].rearrange("p (s c) -> p s c", s=2)
        vtok_st = res[:, 15, :]
        cu, cg, vst, mixt = ws(0), ws(512), [ws(1024), ws(1536)], ws(2048)
        sguw = [ws(2560, 512), ws(3072, 512)]
        hst = [ws(0), ws(512)]
        sq2 = [ws(1024), ws(1536)]
        ot = ws(2048)
        fvar, froot, frstd, fnewt = (part(S0 + 2560 + n * NCH, NCH) for n in range(4))
        q_t, k_t, v_t = ws(0), ws(512), ws(1024)
        v_new, v_cur = ws(1536), ws(2048)
        lsp, sc_t = ws(2560), ws(3072)
        w_t = ws(3584, 2048).rearrange("p (j t) -> p j t", j=NCH)

        dt_x, dt_e, dt_u, dt_l, dt_v, dt_a, dt_cs, dt_w, dt_m = (big[0:HEADS_A, n, :] for n in range(9))
        ea = work[0:HEADS_A, S0:S0 + 1]
        x_tok = big[:, :, :].rearrange("p k t -> p (k t)").rearrange("p (c f) -> p c f", c=NCH)
        b_tok = res[:, 8:12, :]

        acc = [bank("acc0"), bank("acc1")]
        p_tr, p_s0, p_s1, p_y, p_st, p_tv = (bank(n) for n in ("p_tr", "p_s0", "p_s1", "p_y", "p_st", "p_tv"))

        const_landed = sem("const_landed")
        zeros_ready = sem("zeros_ready")
        shapes_landed = sem("shapes_landed")
        x_landed = [sem(f"x_landed{n}") for n in range(len(X_PARTS))]
        w_landed = [sem(f"w_landed{n}") for n in range(RING)]
        w_hi_ready = sem("w_hi_ready")
        w_ready = sem("w_ready")
        w_used = sem("w_used")
        a_hi_ready = sem("a_hi_ready")
        a_ready = sem("a_ready")
        evacuated = sem("evacuated")
        conv_done = sem("conv_done")
        act_done = sem("act_done")
        bc_stored = sem("bc_stored")
        tr_done = sem("tr_done")
        tr_free = sem("tr_free")
        dve_step, act_step, pool_step = sem("dve_step"), sem("act_step"), sem("pool_step")
        sq_ready = sem("sq_ready")
        sum_ready = sem("sum_ready")
        sum_done = sem("sum_done")
        var_ready = sem("var_ready")
        root_ready = sem("root_ready")
        dt_dve, dt_act = sem("dt_dve"), sem("dt_act")
        dt_ready = sem("dt_ready")
        cs_stored = sem("cs_stored")
        z_stored = [sem("z_stored0"), sem("z_stored1")]
        v_stored = sem("v_stored")
        cs_loaded, z_loaded, ya_stored = sem("cs_loaded"), sem("z_loaded"), sem("ya_stored")
        ecs_ready, end_ready, clamp_ready, dec_ready = (sem(n) for n in ("ecs_ready", "end_ready", "clamp_ready", "dec_ready"))
        bst_ready, x_ready, ce_ready, g_ready = (sem(n) for n in ("bst_ready", "x_ready", "ce_ready", "g_ready"))
        scores_done, y_done, states_done, y_gated = (sem(n) for n in ("scores_done", "y_done", "states_done", "y_gated"))
        state_ready = sem("state_ready")
        ysq_ready, ysq_added = sem("ysq_ready"), sem("ysq_added")
        stats_done = sem("stats_done")
        vtok_ready = sem("vtok_ready")
        ln_var, ln_root = sem("ln_var"), sem("ln_root")
        vst_loaded = [sem("vst_loaded0"), sem("vst_loaded1")]
        vnorm_ready = sem("vnorm_ready")
        mixin_ready, mix_done, yb_ready = sem("mixin_ready"), sem("mix_done"), sem("yb_ready")
        h_loaded = [sem("h_loaded0"), sem("h_loaded1")]
        h_ready = sem("h_ready")
        ya_loaded = [sem(f"ya_loaded{n}") for n in range(4)]
        hsq_ready, hsq_added = sem("hsq_ready"), sem("hsq_added")
        g_silu, vtr_done, vtr_copied, v_taken = (sem(n) for n in ("g_silu", "vtr_done", "vtr_copied", "v_taken"))
        z_done, l_ready, e_ready, w_soft = (sem(n) for n in ("z_done", "l_ready", "e_ready", "w_soft"))
        wtr_done, wtr_copied, pv_done, yo_ready = (sem(n) for n in ("wtr_done", "wtr_copied", "pv_done", "yo_ready"))
        fvar_ready, froot_ready, frstd_ready = (sem(n) for n in ("fvar_ready", "froot_ready", "frstd_ready"))
        fsum_done, spread_done, spread_copied = (sem(n) for n in ("fsum_done", "spread_done", "spread_copied"))
        weighted = sem("weighted")
        out_dve, out_pool, out_stored = sem("out_dve"), sem("out_pool"), sem("out_stored")

        def bank_of(t):
            return {2: p_s0, 3: p_s1, T_OO + 2: p_tv}.get(t[0], acc[t[0] % 2]) if t[2] is None else acc[t[0] % 2]

        def lin(t, k=1, c=0):
            first, stride, reg = t
            return k * first + c if reg is None else reg * (k * stride) + (k * first + c)

        def half(t):
            first, stride, reg = t
            return first // 2 if reg is None else reg * (stride // 2) + first // 2

        def at(t, c=0):
            return (t[0] + c, t[1], t[2])

        def slot(t, h):
            return (2 * t[0] + h) % RING

        def tile_of(buf, n):
            return buf[:, n, :] if isinstance(n, int) else buf[:, ds(n, 1), :].rearrange("p a t -> p (a t)")

        def dram_tile(buf, n):
            return buf[n] if isinstance(n, int) else buf[ds(n, 1)].rearrange("a p t -> (a p) t")

        def col(base, n):
            return tab[:, base + n:base + n + 1] if isinstance(n, int) else tab[:, ds(n + base, 1)]

        def ones_row(n):
            return ones[:, 0:1].to_broadcast([P, n])

        class Steps:

            def __init__(self, eng, semaphore):
                self.eng, self.sem, self.base, self.k, self.reg, self.per = eng, semaphore, 0, 0, None, 0

            def __call__(self, ins):
                self.k += 1
                ins.then_inc(self.sem, 1)
                self.eng.wait_ge(self.sem, self.base + self.k if self.reg is None
                                 else self.reg * self.per + (self.base + self.k))

            def loop(self, reg, per):
                self.base, self.k, self.reg, self.per = self.base + self.k, 0, reg, per

            def end(self, trips):
                assert self.k == self.per, f"{self.sem} takes {self.k} steps in a trip, not {self.per}"
                self.base, self.k, self.reg = self.base + self.per * trips, 0, None

        block = ctx.enter_context(nc.Block())

        @block.sync
        def _(sp):
            def load_weights(t, halves=(0, 1)):
                for h in halves:
                    if t[0] >= 2:
                        sp.wait_ge(w_ready, lin(t, 2, h - 3))
                    n = lin(t, 2, h)
                    src = weights[n] if isinstance(n, int) else weights[ds(n, 1)].rearrange("a p n -> (a p) n")
                    sp.dma_start(w_raw[:, slot(t, h), :], src).then_inc(w_landed[slot(t, h)], 16)

            for s in (z_stored[0], z_stored[1], v_stored, ya_stored):
                sp.sem_inc(s, 16)
            sp.dma_start(tab, table).then_inc(const_landed, 16)
            for n, (first, end) in enumerate(X_PARTS):
                sp.dma_start(big[:, first:end, :], xT[first:end].rearrange("k p t -> p k t")).then_inc(x_landed[n], 16)
                if n < 2:
                    load_weights((0, 0, None), (n,))
            sp.dma_start(work[:, 0:640], shapes).then_inc(shapes_landed, 16)
            for n in range(1, 5):
                load_weights((n, 0, None))
            sp.wait_ge(dt_ready, 1)
            sp.dma_start(cs_dram[0:HEADS_A], dt_cs).then_inc(cs_stored, 16)
            sp.dma_start(cs_dram[HEADS_A:HEADS_A + RH], dt_cs[0:RH]).then_inc(cs_stored, 16)
            with sp.Fori(0, (T_Z - T_B) // 2) as i:
                for j in range(2):
                    load_weights((T_B + 4 + j, 2, i))
            with sp.Fori(0, KT // 2) as i:
                for j in range(2):
                    t = (T_Z + j, 2, i)
                    load_weights(at(t, 4))
                    sp.wait_ge(act_done, lin(t))
                    sp.dma_start(dram_tile(z_dram, lin(t, 1, -T_Z)), cv[(T_Z + j) % 2]).then_inc(z_stored[j], 16)
            sp.wait_ge(cs_stored, 32)
            for j in range(2):
                sp.wait_ge(z_stored[j], 16 * (KT // 2) + 16)
            def cs_of(heads, c):
                return cs_dram[heads, c * P:(c + 1) * P].partition_broadcast(P)

            csb3 = csb.rearrange("p (h l) -> p h l", h=RH)
            sp.dma_start(csb3, cs_of(slice(0, RH), 0)).then_inc(cs_loaded, 16)
            with sp.Fori(0, GROUPS) as g:
                for c in range(NCH):
                    t = (T_V + c, NCH, g)
                    k = lin((c, NCH, g))
                    cs_next = cs_of(ds(g * RH + (c + 1) // NCH * RH, RH), (c + 1) % NCH)
                    sp.wait_ge(clamp_ready, k + 1)
                    sp.wait_ge(end_ready, k + 1)
                    sp.dma_start(csb3, cs_next).then_inc(cs_loaded, 16)
                    sp.wait_ge(ya_stored, k * 16 + 16)
                    sp.wait_ge(ysq_ready, k + 1)
                    sp.dma_start(zya.rearrange("p (j l) -> p j l", j=NCH),
                                 z_dram[ds(g * NCH, NCH), :, c * P:(c + 1) * P].rearrange("j p l -> p j l")).then_inc(z_loaded, 16)
                    load_weights(at(t, 4))
                    sp.wait_ge(vtok_ready, k + 1)
                    sp.dma_start(dram_tile(v_dram, k), vtok_st).then_inc(v_stored, 16)
                    sp.wait_ge(y_gated, k + 2)
                    sp.dma_start(ya_dram[ds(g * NCH, NCH), :, c * P:(c + 1) * P].rearrange("j p l -> p j l"),
                                 zya.rearrange("p (j l) -> p j l", j=NCH)).then_inc(ya_stored, 16)
            sp.wait_ge(v_stored, 16 * KT + 16)
            sp.wait_ge(ya_stored, 16 * KT + 16)
            sp.wait_ge(ysq_added, KT + 2)

            def load_mix(n, i):
                sp.dma_start(vst[n], dram_tile(v_dram, i)).then_inc(vst_loaded[n], 16)
                w_src = sgu_wT[i] if isinstance(i, int) else sgu_wT[ds(i, 1)].rearrange("a s t -> (a s) t")
                sp.dma_start(sguw[n][:, 0:P], w_src).then_inc(vst_loaded[n], 16)
                row = sgu_rows[i] if isinstance(i, int) else sgu_rows[ds(i, 1)].rearrange("a n -> (a n)")
                sp.dma_start(sguw[n][:, P:4 * P], row.partition_broadcast(P)).then_inc(vst_loaded[n], 16)

            for n in range(2):
                load_mix(n, n)
            with sp.Fori(0, KT // 2 - 1) as i:
                for n in range(2):
                    for j in range(2):
                        load_weights((T_UG + 4 + 2 * n + j, 4, i))
                    sp.wait_ge(yb_ready, i * 2 + (n + 1))
                    load_mix(n, i * 2 + (n + 2))
            for j in range(4):
                load_weights((T_OB + j, 0, None))
            sp.wait_ge(yb_ready, KT)

            def load_h(n, i):
                sp.dma_start(hst[n], dram_tile(xT, i)).then_inc(h_loaded[n], 16)

            load_h(0, 0)
            load_h(1, 1)
            sp.wait_ge(a_ready, 2 * KT)
            for n in range(4):
                sp.dma_start(big[:, 4 * n:4 * n + 4, :],
                             ya_dram[4 * n:4 * n + 4].rearrange("k p t -> p k t")).then_inc(ya_loaded[n], 16)
            with sp.Fori(0, KT // 2 - 1) as i:
                for j in range(2):
                    load_weights((T_OB + 4 + j, 2, i))
                    sp.wait_ge(h_ready, i * 2 + (j + 1))
                    load_h(j, i * 2 + (j + 2))
            with sp.Fori(0, (T_END - 4 - T_OA + 2) // 2) as i:
                for j in range(2):
                    load_weights((T_OA - 2 + 4 + j, 2, i))
            for f in range(KT):
                by_pool = f in OUT_BY_POOL
                done = sum((n in OUT_BY_POOL) == by_pool for n in range(f + 1))
                sp.wait_ge(out_pool if by_pool else out_dve, done)
                sp.dma_start(out[f], res[:, f, :]).then_inc(out_stored, 16)
            sp.wait_ge(out_stored, 16 * KT)

        @block.scalar
        def _(act):
            A = nc.scalar.activation
            step = Steps(act, act_step)

            def split(t, halves=(0, 1)):
                for h in halves:
                    if t[0] >= T_END:
                        break
                    s = slot(t, h)
                    act.wait_ge(w_landed[s], half(t) * 16 + 16)
                    if t[0] >= 2:
                        act.wait_ge(w_used, lin(t, 2, h - 3))
                    A(w_hi[:, s, :], w_raw[:, s, :], ACT.Copy).then_inc(w_hi_ready, 1)

            def root(n):
                act.wait_ge(var_ready, n)
                A(root_t, var_t, ACT.Sqrt).then_inc(root_ready, 1)

            def high_parts(src, scale_at, first, end):
                for k in range(first, end):
                    if scale_at is None:
                        A(a_hi[:, k, :], src[:, k, :], ACT.Copy).then_inc(a_hi_ready, 1)
                    else:
                        A(a_hi[:, k, :], src[:, k, :], ACT.Identity, scale=col(scale_at, k)).then_inc(a_hi_ready, 1)

            def first_high_parts(src, scale_at, t):
                act.wait_ge(w_used, 2 * t[0] + 1)
                high_parts(src, scale_at, 0, HK)
                split(at(t, 2), (0,))

            for s in (ysq_ready, wtr_copied):
                act.sem_inc(s, 1)
            nc.scalar.preload_act_table_set("sqrt_and_others")
            act.wait_ge(const_landed, 16)
            for n, (first, end) in enumerate(X_PARTS):
                act.wait_ge(x_landed[n], 16)
                for k in range(first, end):
                    A(a_hi[:, k, :], big[:, k, :], ACT.Identity, scale=col(C_NW0, k)).then_inc(a_hi_ready, 1)
                if n < 2:
                    split((0, 0, None), (n,))
            split((1, 0, None))
            for k in range(KT):
                act.wait_ge(a_ready, k + 1)
                A(big[:, k, :], big[:, k, :], ACT.Square).then_inc(sq_ready, 1)
            split((2, 0, None))
            root(1)
            split((3, 0, None))

            def copy_tokens(ordinal, dst):
                act.wait_ge(tr_done, ordinal + 1)
                A(dst, p_tr[:, :].rearrange("p (c f) -> p c f", c=NCH), ACT.Copy).then_inc(tr_free, 1)

            def dt_functions():
                nc.scalar.preload_act_table_set("natural_log_exp_and_others")
                A(ea, tab[0:HEADS_A, C_ALOG:C_ALOG + 1], ACT.Exp).then_inc(dt_act, 1)
                act.wait_ge(dt_dve, 1)
                step(A(dt_e, dt_x, ACT.Abs))
                A(dt_e, dt_e, ACT.Exp, scale=-1.0).then_inc(dt_act, 1)
                act.wait_ge(dt_dve, 2)
                A(dt_l, dt_u, ACT.Ln).then_inc(dt_act, 1)
                act.wait_ge(dt_dve, 3)
                A(dt_w, dt_w, ACT.Exp).then_inc(dt_act, 1)

            for n in range(GROUPS):
                t = (T_B + n, 0, None)
                act.wait_ge(conv_done, t[0])
                A(xs[t[0] % 2], xs[t[0] % 2], ACT.Silu).then_inc(act_done, 1)
                split(at(t, 3))
                if n == 0:
                    dt_functions()
                else:
                    copy_tokens(n - 1, b_tok[:, :, (n - 1) * P:n * P])
            copy_tokens(GROUPS - 1, b_tok[:, :, (GROUPS - 1) * P:])
            for n in range(GROUPS):
                t = (T_C + n, 0, None)
                if n > 0:
                    split(at(t, 2))
                act.wait_ge(conv_done, t[0])
                A(res[:, GROUPS + n, :], xs[t[0] % 2], ACT.Silu).then_inc(act_done, 1)
            act.wait_ge(cs_stored, 32)
            with act.Fori(0, KT // 2) as i:
                for j in range(2):
                    t = (T_X + j, 2, i)
                    split(at(t, 2))
                    act.wait_ge(conv_done, lin(t))
                    A(xs[(T_X + j) % 2], xs[(T_X + j) % 2], ACT.Silu).then_inc(act_done, 1)
                    copy_tokens(lin(t, 1, -4), x_tok[:, :, ds(i * (2 * P) + j * P, P)])
            with act.Fori(0, KT // 2) as i:
                for j in range(2):
                    t = (T_Z + j, 2, i)
                    split(at(t, 2))
                    act.wait_ge(evacuated, lin(t, 1, 1))
                    A(cv[(T_Z + j) % 2], cv[(T_Z + j) % 2], ACT.Silu).then_inc(act_done, 1)
            for j in range(2):
                act.wait_ge(z_stored[j], 16 * (KT // 2) + 16)
            with act.Fori(0, GROUPS) as g:
                for c in range(NCH):
                    t = (T_V + c, NCH, g)
                    k = lin((c, NCH, g))
                    nc.scalar.preload_act_table_set("exp_and_others")
                    act.wait_ge(clamp_ready, k + 1)
                    A(dec, dec, ACT.Exp).then_inc(dec_ready, 1)
                    act.wait_ge(cs_loaded, k * 16 + 16)
                    if c:
                        act.wait_ge(y_done, k + 1)
                        A(ecs, csb, ACT.Exp).then_inc(ecs_ready, 1)
                    act.wait_ge(state_ready, g * 3 + (c + 1))
                    A(end_decay, csb.rearrange("p (h l) -> p h l", h=RH)[:, :, P - 1], ACT.Exp).then_inc(end_ready, 1)
                    split(at(t, 2))
                    act.wait_ge(evacuated, lin(t, 1, 1))
                    A(vcv, vcv, ACT.Gelu_apprx_tanh).then_inc(act_done, 1)
                    act.wait_ge(v_stored, k * 16 + 16)
                    act.wait_ge(stats_done, k + 1)
                    act.wait_ge(tr_done, lin(t, 1, -20 + 1))
                    A(vtok_st, p_tr[:, :], ACT.Copy).then_inc(vtok_ready, 1)
                    act.wait_ge(y_gated, k + 2)
                    act.wait_ge(ysq_added, k + 2)
                    A(ysq, zya, ACT.Square).then_inc(ysq_ready, 1)
            act.wait_ge(ln_var, 1)
            A(vrs[:, 0, :], vrs[:, 1, :], ACT.Sqrt).then_inc(ln_root, 1)
            def u_and_g(tu, last=False):
                tg = at(tu, 1)
                split(at(tu, 2))
                act.wait_ge(evacuated, lin(tu, 1, 1))
                A(cu, cu, ACT.Gelu_apprx_tanh).then_inc(act_done, 1)
                if last:
                    act.wait_ge(yb_ready, HK)
                    first_high_parts(big, None, tg)
                else:
                    split(at(tg, 2))
                act.wait_ge(evacuated, lin(tg, 1, 1))
                A(cg, cg, ACT.Silu).then_inc(act_done, 1)

            with act.Fori(0, KT // 2 - 1) as i:
                for n in range(2):
                    u_and_g((T_UG + 2 * n, 4, i))
            u_and_g((T_OB - 4, 0, None))
            u_and_g((T_OB - 2, 0, None), True)
            act.wait_ge(w_used, 2 * T_OB)
            act.wait_ge(yb_ready, KT - 1)
            high_parts(big, None, HK, KT - 1)
            act.wait_ge(yb_ready, KT)
            high_parts(big, None, KT - 1, KT)
            split((T_OB + 1, 0, None), (1,))
            root(2)
            with act.Fori(0, KT // 2 - 1) as i:
                for j in range(2):
                    split((T_OB + 2 + j, 2, i))
            split((T_OA, 0, None))
            for n in range(2):
                act.wait_ge(ya_loaded[n], 16)
            first_high_parts(big, C_SSDW, (T_OA - 1, 0, None))
            act.wait_ge(w_used, 2 * T_OA)
            for n in range(2, 4):
                act.wait_ge(ya_loaded[n], 16)
            high_parts(big, C_SSDW, HK, KT)
            split((T_OA + 1, 0, None), (1,))

            def square_h(par, f, ready, added):
                act.wait_ge(h_ready, ready)
                if added is not None:
                    act.wait_ge(hsq_added, added)
                A(sq2[par], tile_of(res, f), ACT.Square).then_inc(hsq_ready, 1)

            for j in range(2):
                split((T_OA + 2 + j, 0, None))
                square_h(j, j, KT + j + 1, None)
            with act.Fori(1, KT // 2 - 1) as i:
                for j in range(2):
                    split((T_OA + 2 + j, 2, i))
                    square_h(j, i * 2 + j, i * 2 + (KT + j + 1), i * 2 + (j - 1))
            split((T_AT, 0, None))
            square_h(0, KT - 2, 2 * KT - 1, KT - 3)
            first_high_parts(res, C_NW1, (T_AT - 1, 0, None))
            act.wait_ge(w_used, 2 * T_AT)
            high_parts(res, C_NW1, HK, KT - 1)
            act.wait_ge(h_ready, 2 * KT)
            high_parts(res, C_NW1, KT - 1, KT)
            square_h(1, KT - 1, 2 * KT, KT - 2)
            split((T_AT + 1, 0, None), (1,))

            def softplus(j, h1):
                zb, n = (p_s1 if j == 1 else p_s0), (T if j == 2 else 3 * P)
                act.wait_ge(z_done, h1 * 3 + (j + 1))
                step(A(lsp[:, 0:n], zb[:, 0:n], ACT.Abs))
                step(A(lsp[:, 0:n], lsp[:, 0:n], ACT.Exp, scale=-1.0))
                A(lsp[:, 0:n], lsp[:, 0:n], ACT.Ln, bias=1.0).then_inc(l_ready, 1)

            def weigh(j, h1):
                n = T if j == 2 else 3 * P
                act.wait_ge(e_ready, h1 * 3 + (j + 2))
                A(sc_t[:, 0:n], sc_t[:, 0:n], ACT.Exp).then_inc(w_soft, 1)

            def copy_weights(j, h1):
                act.wait_ge(wtr_done, h1 * 3 + (j + 2))
                src = p_tr[:, :].rearrange("p (j t) -> p j t", j=NCH)
                if j == 0:
                    act.wait_ge(pv_done, h1 + 1)
                    step(A(w_t[:, 0, 0:P], src[:, 0, :], ACT.Copy))
                    A(w_t[:, 0:2, P:2 * P], src[:, 1:3, :], ACT.Copy).then_inc(wtr_copied, 1)
                else:
                    A(w_t[:, 0:j + 2, (j + 1) * P:(j + 2) * P], src[:, 0:j + 2, :], ACT.Copy).then_inc(wtr_copied, 1)

            def silu_g(t, h):
                act.wait_ge(evacuated, lin(t, 1, 2))
                A(tile_of(big, h), tile_of(big, h), ACT.Silu).then_inc(g_silu, 1)

            def head(t, h, attend, slots=4):
                if attend:
                    nc.scalar.preload_act_table_set("natural_log_exp_and_others")
                for j in range(slots):
                    if attend and j < 3:
                        softplus(j, h - 1)
                    split(at(t, j + 2))
                    if attend and j < 3:
                        weigh(j, h - 1)
                    if j == 3:
                        silu_g(t, h)
                    if j == 0:
                        act.wait_ge(vtr_done, h + 1)
                        if attend:
                            act.wait_ge(v_taken, h)
                        A(v_new, p_tv[:, :], ACT.Copy).then_inc(vtr_copied, 1)
                    if attend and j < 3:
                        copy_weights(j, h - 1)

            root(3)
            head((T_AT, 0, None), 0, False)
            with act.Fori(1, HEADS_C - 1) as h:
                step.loop(h - 1, 7)
                head((T_AT, 4, h), h, True)
            step.end(HEADS_C - 2)
            last = HEADS_C - 1
            t = (T_AT + 4 * last, 0, None)
            head(t, last, True, 2)
            softplus(2, last - 1)
            split(at(t, 4))
            act.wait_ge(w_used, 2 * T_OO - 1)
            act.wait_ge(yo_ready, last)
            high_parts(big, None, 0, 4)
            weigh(2, last - 1)
            high_parts(big, None, 4, 6)
            copy_weights(2, last - 1)
            high_parts(big, None, 6, HK)
            split(at(t, 5), (0,))
            act.wait_ge(w_used, 2 * T_OO)
            high_parts(big, None, HK, last - 1)
            act.wait_ge(yo_ready, last + 1)
            high_parts(big, None, last - 1, last)
            softplus(0, last)
            split(at(t, 5), (1,))
            weigh(0, last)
            split(at(t, 6), (0,))
            copy_weights(0, last)
            softplus(1, last)
            weigh(1, last)
            copy_weights(1, last)
            softplus(2, last)
            weigh(2, last)
            copy_weights(2, last)
            silu_g(t, last)
            nc.scalar.preload_act_table_set("sqrt_and_others")
            act.wait_ge(yo_ready, HEADS_C + 1)
            high_parts(big, None, last, KT)
            split(at(t, 6), (1,))
            for f in range(KT):
                if f > 0:
                    split((T_OO + 2 + f, 0, None))
                square_h(f % 2, f, 2 * KT + f + 1, KT + f - 1)
                if f in OUT_BY_POOL:
                    A(res[:, f, :], res[:, f, :], ACT.Identity, scale=col(C_FNW, f)).then_inc(weighted, 1)
            act.wait_ge(fvar_ready, 1)
            A(froot, fvar, ACT.Sqrt).then_inc(froot_ready, 1)
            act.wait_ge(spread_done, 2)
            A(rstd, p_s0[:, :], ACT.Copy).then_inc(spread_copied, 1)

        @block.gpsimd
        def _(pool):
            TT = nc.gpsimd.tensor_tensor
            step = Steps(pool, pool_step)
            pool.wait_ge(shapes_landed, 16)
            for n in range(GROUPS):
                pool.wait_ge(act_done, T_B + n)
                nc.gpsimd.tensor_copy(res[:, n, :], xs[(T_B + n) % 2]).then_inc(bc_stored, 1)
            pool.wait_ge(sum_done, 1)
            nc.gpsimd.memset(ssum, 0.0).then_inc(ysq_added, 1)
            pool.wait_ge(act_done, T_Z - 1)
            pool.wait_ge(tr_free, T_Z - 4)
            for j in range(2):
                pool.wait_ge(z_stored[j], 16 * (KT // 2) + 16)

            def add_squares(c):
                chunk = slice(c * P, (c + 1) * P)
                for j in range(NCH):
                    ins = TT(ssum[:, chunk], ssum[:, chunk], ysq[:, j * P:(j + 1) * P], ALU.add)
                    if j < NCH - 1:
                        step(ins)
                ins.then_inc(ysq_added, 1)

            step(nc.gpsimd.memset(ysq, 0.0))
            with pool.Fori(0, GROUPS) as g:
                step.loop(g, NCH * (NCH - 1))
                for c in range(NCH):
                    k = lin((c, NCH, g))
                    hs, chunk = ds(g * RH, RH), slice(c * P, (c + 1) * P)
                    pool.wait_ge(scores_done, k + 1)
                    TT(b_st, tile_of(res, g)[:, chunk], ones, ALU.mult).then_inc(bst_ready, 1)
                    xc = x_tok[:, c, ds(g * T, T)]
                    pool.wait_ge(y_done, k + 1)
                    TT(x_st, xc, ones_row(T), ALU.mult).then_inc(x_ready, 1)
                    pool.wait_ge(states_done, g * 3 + (c + 1))
                    TT(bt_st, b_tok[:, c, ds(g * P, P)], ones, ALU.mult).then_inc(bst_ready, 1)
                    TT(xw.rearrange("p (h d) -> p h d", h=RH), xc.rearrange("p (h d) -> p h d", h=RH),
                       tok[:, 2, c, hs].unsqueeze(2).to_broadcast([P, RH, PD]), ALU.mult).then_inc(x_ready, 1)
                    pool.wait_ge(ysq_ready, k + 1)
                    add_squares((c - 1) % NCH)
                    if c:
                        pool.wait_ge(ysq_added, k + 2)
                        pool.wait_ge(ecs_ready, g * 3 + c)
                        ecs3 = ecs.rearrange("p (h l) -> p h l", h=RH)
                        TT(ecs3, ecs3, tile_of(res, g + GROUPS)[:, chunk].unsqueeze(1).to_broadcast([P, RH, P]),
                           ALU.mult).then_inc(ce_ready, 1)
            step.end(GROUPS)
            pool.wait_ge(ysq_ready, KT + 1)
            add_squares(NCH - 1)
            with pool.Fori(0, KT // 2) as i:
                step.loop(i, 2)
                for n in range(2):
                    pool.wait_ge(vst_loaded[n], i * 48 + 48)
                    TT(sguw[n][:, 0:P], sguw[n][:, 0:P], causal, ALU.mult).then_inc(mixin_ready, 1)
                    v3 = vst[n].rearrange("p (c f) -> p c f", c=NCH)
                    pool.wait_ge(vnorm_ready, i * 2 + (n + 1))
                    step(TT(v3, v3, sguw[n][:, P:2 * P].unsqueeze(1).to_broadcast([P, NCH, P]), ALU.mult))
                    TT(v3, v3, sguw[n][:, 2 * P:3 * P].unsqueeze(1).to_broadcast([P, NCH, P]), ALU.add).then_inc(mixin_ready, 1)
            step.end(KT // 2)

            pool.wait_ge(sum_done, 2)
            step(nc.gpsimd.memset(ssum, 0.0))
            with pool.Fori(0, KT // 2) as i:
                step.loop(i, 2)
                for j in range(2):
                    pool.wait_ge(hsq_ready, i * 2 + (j + 1))
                    step(TT(ssum, ssum, sq2[j], ALU.add))
                    pool.sem_inc(hsq_added, 1)
            step.end(KT // 2)
            pool.wait_ge(sum_done, 3)
            step(nc.gpsimd.memset(ssum, 0.0))
            pool.wait_ge(vtr_copied, 1)
            TT(v_cur, v_new, ones_row(T), ALU.mult).then_inc(v_taken, 1)
            with pool.Fori(1, HEADS_C) as h:
                pool.wait_ge(vtr_copied, h + 1)
                pool.wait_ge(pv_done, h + 1)
                TT(v_cur, v_new, ones_row(T), ALU.mult).then_inc(v_taken, 1)
            for f in range(KT - 1):
                pool.wait_ge(hsq_ready, KT + f + 1)
                step(TT(ssum, ssum, sq2[f % 2], ALU.add))
                pool.sem_inc(hsq_added, 1)
            pool.wait_ge(spread_copied, 1)
            pool.wait_ge(weighted, len(OUT_BY_POOL))
            for f in OUT_BY_POOL:
                TT(res[:, f, :], res[:, f, :], rstd, ALU.mult).then_inc(out_pool, 1)

        @block.vector
        def _(dve):
            V = nc.vector
            step = Steps(dve, dve_step)

            def split(t, halves=(0, 1)):
                for h in halves:
                    if t[0] >= T_END:
                        break
                    s = slot(t, h)
                    dve.wait_ge(w_hi_ready, lin(t, 2, h + 1))
                    V.tensor_tensor(w_lo[:, s, :], w_raw[:, s, :], w_hi[:, s, :].bitcast(F32),
                                    ALU.subtract).then_inc(w_ready, 1)

            def low_parts(src, scale_at, n, first, end):
                for k in range(first, end):
                    dve.wait_ge(a_hi_ready, n * KT + k + 1)
                    hi = a_hi[:, k, :].bitcast(F32)
                    if scale_at is None:
                        V.tensor_tensor(a_lo[:, k, :], src[:, k, :], hi, ALU.subtract).then_inc(a_ready, 1)
                    else:
                        V.scalar_tensor_tensor(a_lo[:, k, :], src[:, k, :], col(scale_at, k), hi,
                                               ALU.mult, ALU.subtract).then_inc(a_ready, 1)

            def first_low_parts(src, scale_at, n, t):
                dve.wait_ge(w_used, 2 * t[0] + 1)
                low_parts(src, scale_at, n, 0, HK)
                split(at(t, 2), (0,))

            def inverse_root(n):
                dve.wait_ge(sum_done, n)
                V.tensor_scalar(var_t, p_st[:, :], 1.0 / D, EPS, ALU.mult, ALU.add).then_inc(var_ready, 1)
                dve.wait_ge(root_ready, n)
                step(V.reciprocal(rstd, root_t))
                step(V.tensor_tensor(newt_t, rstd, rstd, ALU.mult))
                step(V.tensor_tensor(newt_t, newt_t, var_t, ALU.mult))
                step(V.tensor_scalar(newt_t, newt_t, -0.5, 1.5, ALU.mult, ALU.add))
                step(V.tensor_tensor(rstd, rstd, newt_t, ALU.mult))

            def evacuate(t, dst):
                dve.wait_ge(w_used, lin(t, 2, 2))
                V.tensor_tensor(dst, bank_of(t)[:, :], rstd, ALU.mult).then_inc(evacuated, 1)

            for s in (state_ready, e_ready, yo_ready, g_ready, y_gated, stats_done):
                dve.sem_inc(s, 1)
            V.memset(zeros, 0.0).then_inc(zeros_ready, 1)
            dve.wait_ge(const_landed, 16)
            for n, (first, end) in enumerate(X_PARTS):
                low_parts(big, C_NW0, 0, first, end)
                if n < 2:
                    split((0, 0, None), (n,))
            split((1, 0, None))
            dve.wait_ge(sq_ready, 2)
            step(V.tensor_tensor(ssum, big[:, 0, :], big[:, 1, :], ALU.add))
            for k in range(2, KT):
                dve.wait_ge(sq_ready, k + 1)
                ins = V.tensor_tensor(ssum, ssum, big[:, k, :], ALU.add)
                if k < KT - 1:
                    step(ins)
                else:
                    ins.then_inc(sum_ready, 1)
            split((2, 0, None))
            inverse_root(1)
            split((3, 0, None))

            dve.wait_ge(w_used, 2)
            V.tensor_tensor(dt_x, acc[0][0:HEADS_A, :], rstd[0:HEADS_A, :], ALU.mult).then_inc(evacuated, 1)

            def conv(t, n, waits):
                j = t[0] % 2
                evacuate(t, cv[j])
                dve.wait_ge(evacuated, lin(t, 1, 1))
                for s, value in waits:
                    dve.wait_ge(s, value)
                step(V.tensor_scalar(xs[j], cv[j], cw(n, 3), cb(n), ALU.mult, ALU.add))
                for d in (1, 2, 3):
                    ins = V.scalar_tensor_tensor(xs[j][:, d:T], cv[j][:, 0:T - d], cw(n, 3 - d), xs[j][:, d:T],
                                                 ALU.mult, ALU.add)
                    if d < 3:
                        step(ins)
                    else:
                        ins.then_inc(conv_done, 1)

            def cw(n, tap):
                return tab[:, C_CW + 4 * n + tap:C_CW + 4 * n + tap + 1] if isinstance(n, int) else tab[:, ds(n * 4 + (C_CW + tap), 1)]

            def cb(n):
                return col(C_CB, n)

            def dt_and_decays():
                dve.wait_ge(evacuated, 1)
                V.tensor_scalar(dt_x, dt_x, tab[0:HEADS_A, C_DTB:C_DTB + 1], None, ALU.add).then_inc(dt_dve, 1)
                step(V.memset(dt_m, 1.0))
                step(V.memset(dt_m.rearrange("p (c l) -> p c l", c=NCH)[:, :, 0:1], 0.0))
                dve.wait_ge(dt_act, 2)
                V.tensor_scalar(dt_u, dt_e, 1.0, None, ALU.add).then_inc(dt_dve, 1)
                dve.wait_ge(dt_dve, 2)
                step(V.tensor_scalar(dt_v, dt_u, -1.0, None, ALU.add))
                step(V.tensor_tensor(dt_v, dt_e, dt_v, ALU.subtract))
                dve.wait_ge(dt_act, 3)
                step(V.tensor_tensor(dt_l, dt_l, dt_v, ALU.add))
                step(V.scalar_tensor_tensor(dt_v, dt_x, 0.0, dt_l, ALU.max, ALU.add))
                step(V.tensor_scalar(dt_a, dt_v, ea, -1.0, ALU.mult, ALU.mult))
                V.tensor_tensor_scan(dt_cs, dt_m, dt_a, 0.0, ALU.mult, ALU.add).then_inc(dt_ready, 1)
                dve.wait_ge(dt_ready, 1)
                cs3 = dt_cs.rearrange("p (c l) -> p c l", c=NCH)
                V.tensor_tensor(dt_w.rearrange("p (c l) -> p c l", c=NCH), cs3[:, :, P - 1:P].to_broadcast([HEADS_A, NCH, P]),
                                cs3, ALU.subtract).then_inc(dt_dve, 1)
                dve.wait_ge(dt_act, 4)
                V.tensor_tensor(dt_w, dt_w, dt_v, ALU.mult).then_inc(dt_ready, 1)

            for n in range(GROUPS):
                t = (T_B + n, 0, None)
                conv(t, n, [(tr_done, n - 1), (bc_stored, n - 1)] if n >= 2 else [])
                split(at(t, 3))
                if n == 0:
                    dt_and_decays()
            for n in range(GROUPS):
                t = (T_C + n, 0, None)
                if n > 0:
                    split(at(t, 2))
                conv(t, GROUPS + n, [(tr_done, GROUPS), (bc_stored, GROUPS), (act_done, t[0] - 2)])
            dve.wait_ge(tr_done, GROUPS + 1)
            V.tensor_copy(work[:, 860:860 + 384], p_tr[:, 0:384]).then_inc(tr_free, 1)
            with dve.Fori(0, KT // 2) as i:
                step.loop(i, 6)
                for j in range(2):
                    t = (T_X + j, 2, i)
                    split(at(t, 2))
                    conv(t, lin(t, 1, -1), [(act_done, lin(t, 1, -2)), (tr_done, lin(t, 1, -5))])
            step.end(KT // 2)
            with dve.Fori(0, KT // 2) as i:
                for j in range(2):
                    t = (T_Z + j, 2, i)
                    split(at(t, 2))
                    dve.wait_ge(z_stored[j], i * 16 + 16)
                    evacuate(t, cv[(T_Z + j) % 2])
            dve.wait_ge(shapes_landed, 16)
            state3 = state.rearrange("p (h d) -> p h d", h=RH)
            end3 = end_decay.unsqueeze(2).to_broadcast([P, RH, PD])
            for j in range(2):
                dve.wait_ge(z_stored[j], 16 * (KT // 2) + 16)
            with dve.Fori(0, GROUPS) as g:
                step.loop(g, 10)
                for c in range(NCH):
                    t = (T_V + c, NCH, g)
                    k = lin((c, NCH, g))
                    dve.wait_ge(cs_loaded, k * 16 + 16)
                    for h in range(RH):
                        ins = V.tensor_scalar(dec[:, h * P:(h + 1) * P], csb[:, h * P:(h + 1) * P],
                                              tok[:, 0, c, ds(g * RH + h, 1)], 0.0, ALU.subtract, ALU.min)
                    ins.then_inc(clamp_ready, 1)
                    dve.wait_ge(tr_done, lin(t, 1, -20))
                    evacuate(t, vcv)
                    dve.wait_ge(scores_done, k + 2)
                    step(V.tensor_tensor(smask, p_s0[:, 0:P], causal, ALU.mult))
                    dve.wait_ge(dec_ready, k + 1)
                    for h in range(RH):
                        dec_h = dec[:, h * P:(h + 1) * P]
                        ins = V.scalar_tensor_tensor(dec_h, dec_h, tok[:, 1, c, ds(g * RH + h, 1)], smask, ALU.mult, ALU.mult)
                    step(ins)
                    for h in range(RH):
                        dec_h = dec[:, h * P:(h + 1) * P]
                        ins = V.scalar_tensor_tensor(dec_h, ident, tab[:, ds(g * RH + (C_D + h), 1)], dec_h, ALU.mult, ALU.add)
                    ins.then_inc(g_ready, 1)
                    split(at(t, 2))
                    dve.wait_ge(vtok_ready, k + 1)
                    for q in range(NCH):
                        dst = stats_flat(q, k)
                        ins = V.bn_stats(dst, vtok_st[:, q * P:(q + 1) * P])
                    ins.then_inc(stats_done, 1)
                    dve.wait_ge(y_done, k + 2)
                    dve.wait_ge(z_loaded, k * 16 + 16)
                    V.tensor_tensor(zya, p_y[:, :], zya, ALU.mult).then_inc(y_gated, 1)
                    if c < NCH - 1:
                        dve.wait_ge(states_done, g * 3 + (c + 2))
                        if c == 0:
                            V.tensor_copy(state, p_st[:, :]).then_inc(state_ready, 1)
                        else:
                            dve.wait_ge(end_ready, k + 1)
                            step(V.tensor_tensor(state3, state3, end3, ALU.mult))
                            V.tensor_tensor(state, state, p_st[:, :], ALU.add).then_inc(state_ready, 1)
            step.end(GROUPS)
            dve.wait_ge(cs_loaded, 16 * KT + 16)
            dve.wait_ge(stats_done, KT + 1)
            for c in range(NCH):
                step(V.bn_aggr(mv[:, c, :], stats[:, c, :, :]))
            V.tensor_scalar(vrs[:, 1, :], mv[:, :, 1], EPS, None, ALU.add).then_inc(ln_var, 1)
            dve.wait_ge(ln_root, 1)
            V.reciprocal(vrs[:, 1, :], vrs[:, 0, :]).then_inc(ln_root, 1)
            dve.wait_ge(ln_root, 2)
            def mixed_tile(n, i, tu, last=False):
                tg = at(tu, 1)
                dve.wait_ge(vst_loaded[n], i * 48 + 48)
                for c in range(NCH):
                    v_c = vst[n][:, c * P:(c + 1) * P]
                    ins = V.tensor_scalar(v_c, v_c, mv[:, c, 0:1], vrs[:, 1, c:c + 1], ALU.subtract, ALU.mult)
                ins.then_inc(vnorm_ready, 1)
                split(at(tu, 2))
                evacuate(tu, cu)
                if last:
                    first_low_parts(big, None, 1, tg)
                else:
                    split(at(tg, 2))
                evacuate(tg, cg)
                dve.wait_ge(mix_done, i * 2 + (n + 1))
                step(V.tensor_tensor(mixt.rearrange("p (c l) -> p c l", c=NCH), p_y[:, :].rearrange("p (c l) -> p c l", c=NCH),
                                     sguw[n][:, 3 * P:4 * P].unsqueeze(1).to_broadcast([P, NCH, P]), ALU.add))
                dve.wait_ge(act_done, lin(tg))
                step(V.tensor_tensor(mixt, mixt, cu, ALU.mult))
                V.tensor_tensor(tile_of(big, i * 2 + n), mixt, cg, ALU.mult).then_inc(yb_ready, 1)

            with dve.Fori(0, KT // 2 - 1) as i:
                step.loop(i, 4)
                for n in range(2):
                    mixed_tile(n, i, (T_UG + 2 * n, 4, i))
            step.end(KT // 2 - 1)
            mixed_tile(0, KT // 2 - 1, (T_OB - 4, 0, None))
            mixed_tile(1, KT // 2 - 1, (T_OB - 2, 0, None), True)
            dve.wait_ge(yb_ready, KT)
            low_parts(big, None, 1, HK, KT)
            split((T_OB + 1, 0, None), (1,))
            inverse_root(2)

            def first_sum(j, i, t):
                dve.wait_ge(w_used, lin(t, 2, 2))
                dve.wait_ge(h_loaded[j], i * 16 + 16)
                V.tensor_tensor(tile_of(res, i * 2 + j), acc[t[0] % 2][:, :], hst[j], ALU.add).then_inc(h_ready, 1)
                dve.wait_ge(h_ready, i * 2 + (j + 1))
                dve.sem_inc(evacuated, 1)

            with dve.Fori(0, KT // 2 - 1) as i:
                for j in range(2):
                    t = (T_OB + j, 2, i)
                    split(at(t, 2))
                    first_sum(j, i, t)
            split((T_OA, 0, None))
            first_sum(0, KT // 2 - 1, (T_OA - 2, 0, None))
            first_low_parts(big, C_SSDW, 2, (T_OA - 1, 0, None))
            first_sum(1, KT // 2 - 1, (T_OA - 1, 0, None))
            low_parts(big, C_SSDW, 2, HK, KT)
            split((T_OA + 1, 0, None), (1,))

            def second_sum(j, i, t):
                evacuate(t, ot)
                dve.wait_ge(evacuated, lin(t, 1, 1))
                V.tensor_tensor(tile_of(res, i * 2 + j), tile_of(res, i * 2 + j), ot, ALU.add).then_inc(h_ready, 1)

            with dve.Fori(0, KT // 2 - 1) as i:
                for j in range(2):
                    t = (T_OA + j, 2, i)
                    split(at(t, 2))
                    second_sum(j, i, t)
            split((T_AT, 0, None))
            second_sum(0, KT // 2 - 1, (T_AT - 2, 0, None))
            dve.wait_ge(h_ready, 2 * KT - 1)
            first_low_parts(res, C_NW1, 3, (T_AT - 1, 0, None))
            second_sum(1, KT // 2 - 1, (T_AT - 1, 0, None))
            dve.wait_ge(h_ready, 2 * KT)
            low_parts(res, C_NW1, 3, HK, KT)
            split((T_AT + 1, 0, None), (1,))
            inverse_root(3)

            def soft(j, h1):
                zb, n = (p_s1 if j == 1 else p_s0), (T if j == 2 else 3 * P)
                blocks = [(0, P), (P, 3 * P)] if j == 0 else [(0, n)]
                dve.wait_ge(l_ready, h1 * 3 + (j + 1))
                step(V.scalar_tensor_tensor(lsp[:, 0:n], zb[:, 0:n], 0.0, lsp[:, 0:n], ALU.max, ALU.add))
                for _, end in blocks:
                    step(V.tensor_tensor(lsp[:, end - P:end], lsp[:, end - P:end], strict, ALU.mult))
                dve.wait_ge(wtr_done, h1 * 3 + (j + 1))
                for start, end in blocks:
                    step(V.tensor_tensor_scan(sc_t[:, start:end][:, ::-1], ones_row(end - start), lsp[:, start:end][:, ::-1],
                                              0.0, ALU.mult, ALU.add))
                step(V.tensor_tensor(sc_t[:, 0:n], zb[:, 0:n], sc_t[:, 0:n], ALU.subtract))
                for b, (_, end) in enumerate(blocks):
                    ins = V.tensor_tensor(sc_t[:, end - P:end], sc_t[:, end - P:end], negmask, ALU.add)
                    if b < len(blocks) - 1:
                        step(ins)
                    else:
                        ins.then_inc(e_ready, 1)

            def gate(h1):
                dve.wait_ge(pv_done, h1 + 2)
                dve.wait_ge(g_silu, h1 + 1)
                V.tensor_tensor(tile_of(big, h1), p_y[:, :], tile_of(big, h1), ALU.mult).then_inc(yo_ready, 1)

            def take_q_k(tj, j, h, attend):
                if attend:
                    dve.wait_ge(z_done, h * 3)
                dve.wait_ge(w_used, lin(tj, 2, 2))
                V.scalar_tensor_tensor(q_t if j == 2 else k_t, acc[tj[0] % 2][:, :], P ** -0.5 if j == 2 else 1.0, rstd,
                                       ALU.mult, ALU.mult).then_inc(evacuated, 1)

            def head(t, h, attend, slots=4):
                for j in range(slots):
                    tj = at(t, j)
                    split(at(tj, 2))
                    if j == 0:
                        if attend:
                            dve.wait_ge(vtr_done, h)
                        evacuate(tj, v_t)
                    elif j == 1:
                        evacuate(tj, tile_of(big, h))
                    else:
                        take_q_k(tj, j, h, attend)
                    if attend:
                        soft(j, h - 1) if j < 3 else gate(h - 1)

            head((T_AT, 0, None), 0, False)
            with dve.Fori(1, HEADS_C - 1) as h:
                step.loop(h - 1, 15)
                head((T_AT, 4, h), h, True)
            step.end(HEADS_C - 2)
            last = HEADS_C - 1
            t = (T_AT + 4 * last, 0, None)
            head(t, last, True, 3)
            low_parts(big, None, 4, 0, HK)
            take_q_k(at(t, 3), 3, last, True)
            split(at(t, 5), (0,))
            gate(last - 1)
            low_parts(big, None, 4, HK, last)
            soft(0, last)
            split(at(t, 5), (1,))
            split(at(t, 6), (0,))
            soft(1, last)
            soft(2, last)
            gate(last)
            dve.wait_ge(yo_ready, HEADS_C + 1)
            low_parts(big, None, 4, last, KT)
            split(at(t, 6), (1,))
            for f in range(KT):
                t = (T_OO + f, 0, None)
                if f > 0:
                    split(at(t, 2))
                dve.wait_ge(w_used, lin(t, 2, 2))
                V.tensor_tensor(res[:, f, :], res[:, f, :], bank_of(t)[:, :], ALU.add).then_inc(h_ready, 1)
                dve.wait_ge(h_ready, 2 * KT + f + 1)
                dve.sem_inc(evacuated, 1)
            dve.wait_ge(fsum_done, 1)
            step(V.tensor_scalar(fvar, p_st[:, 0:NCH], 1.0 / D, EPS, ALU.mult, ALU.add))
            dve.wait_ge(fsum_done, 2)
            V.scalar_tensor_tensor(fvar, p_tv[:, 0:NCH], 1.0 / D, fvar, ALU.mult, ALU.add).then_inc(fvar_ready, 1)
            dve.wait_ge(froot_ready, 1)
            step(V.reciprocal(frstd, froot))
            step(V.tensor_tensor(fnewt, fvar, frstd, ALU.mult))
            step(V.scalar_tensor_tensor(fnewt, fnewt, -0.5, frstd, ALU.mult, ALU.mult))
            V.scalar_tensor_tensor(frstd, fnewt, 1.5, frstd, ALU.add, ALU.mult).then_inc(frstd_ready, 1)
            dve.wait_ge(spread_done, 1)
            for f in range(KT):
                if f not in OUT_BY_POOL:
                    V.scalar_tensor_tensor(res[:, f, :], res[:, f, :], col(C_FNW, f), p_y[:, :], ALU.mult, ALU.mult).then_inc(out_dve, 1)

        @block.tensor
        def _(pe):
            M = nc.tensor.matmul

            def products(t, k, first_of=None, behind=None):
                out_t, s, cols = bank_of(t), slot(t, k // HK), slice(k % HK * P, (k % HK + 1) * P)
                if first_of is not None:
                    pe.wait_ge(a_ready, first_of * KT + k + 1)
                ins = M(out_t[:, :], w_hi[:, s, cols], a_hi[:, k, :], start=(k == 0), stop=False)
                if behind is not None:
                    ins.then_inc(behind, 1)
                M(out_t[:, :], w_hi[:, s, cols], a_lo[:, k, :], start=False, stop=False)
                return M(out_t[:, :], w_lo[:, s, cols], a_hi[:, k, :], start=False, stop=(k == KT - 1))

            def project(t, first_of=None):
                if t[0] in (T_B + 3, T_C):
                    pe.wait_ge(evacuated, t[0] - 3)
                elif t[0] > 3:
                    pe.wait_ge(evacuated, lin(t, 1, -1))
                for h in range(2):
                    pe.wait_ge(w_ready, lin(t, 2, h + 1))
                    for kk in range(HK):
                        ins = products(t, h * HK + kk, first_of)
                    ins.then_inc(w_used, 1)

            def sum_squares():
                M(p_st[:, :], ones, ssum, start=True, stop=True).then_inc(sum_done, 1)

            def transposes(src, ordinal):
                if not (isinstance(ordinal, int) and ordinal == 0):
                    pe.wait_ge(tr_free, ordinal)
                for c in range(NCH):
                    ins = nc.tensor.transpose(p_tr[:, c * P:(c + 1) * P], src[:, c * P:(c + 1) * P], ident)
                ins.then_inc(tr_done, 1)

            for s in (scores_done, states_done, y_done, wtr_done, pv_done):
                pe.sem_inc(s, 1)
            pe.wait_ge(zeros_ready, 1)
            for _ in range(4):
                M(p_st[:, :], zeros[:, 0:P], zeros, start=True, stop=True)
            project((0, 0, None), 0)
            project((1, 0, None))
            pe.wait_ge(sum_ready, 1)
            pe.wait_ge(shapes_landed, 16)
            sum_squares()
            project((T_B + 1, 0, None))
            for n in range(GROUPS):
                t = (T_B + n, 0, None)
                project(at(t, 2))
                pe.wait_ge(act_done, t[0])
                transposes(xs[t[0] % 2], n)
            for n in range(2, GROUPS + 1):
                project((T_C + n, 0, None))
            pe.wait_ge(dt_ready, 2)
            pe.wait_ge(tr_free, GROUPS)
            for q, src in enumerate((dt_cs, dt_v, dt_w)):
                for c in range(NCH):
                    o = (q * NCH + c) * HEADS_A
                    ins = nc.tensor.transpose(p_tr[:, o:o + HEADS_A], src[:, c * P:(c + 1) * P], ident[0:HEADS_A, 0:HEADS_A])
            ins.then_inc(tr_done, 1)
            with pe.Fori(0, KT // 2) as i:
                for j in range(2):
                    t = (T_X + j, 2, i)
                    project(at(t, 1))
                    pe.wait_ge(act_done, lin(t))
                    transposes(xs[(T_X + j) % 2], lin(t, 1, -4))
            with pe.Fori(0, KT // 2) as i:
                for j in range(2):
                    project((T_Z + j + 1, 2, i))
            with pe.Fori(0, GROUPS) as g:
                for c in range(NCH):
                    t = (T_V + c, NCH, g)
                    k = lin((c, NCH, g))
                    pe.wait_ge(bst_ready, k * 2 + 1)
                    pe.wait_ge(g_ready, k + 1)
                    M(p_s0[:, 0:P], b_st, tile_of(res, g + GROUPS)[:, c * P:(c + 1) * P], start=True, stop=True).then_inc(scores_done, 1)
                    project(at(t, 1))
                    pe.wait_ge(act_done, lin(t))
                    for q in range(NCH):
                        ins = nc.tensor.transpose(p_tr[:, q * P:(q + 1) * P], vcv[:, q * P:(q + 1) * P], ident)
                    ins.then_inc(tr_done, 1)
                    pe.wait_ge(g_ready, k + 2)
                    pe.wait_ge(x_ready, k * 2 + 1)
                    pe.wait_ge(y_gated, k + 1)
                    if c:
                        pe.wait_ge(ce_ready, g * 3 + c)
                        pe.wait_ge(state_ready, g * 3 + (c + 1))
                    for j in range(NCH):
                        cols = slice(j * P, (j + 1) * P)
                        pair = [(2 * j + a, p_y[PD * a:PD * (a + 1), cols]) for a in range(2)]
                        for r, o in pair:
                            ins = M(o, x_st[:, r * PD:(r + 1) * PD], dec[:, r * P:(r + 1) * P], start=True,
                                    stop=(c == 0), skip_group_check=True)
                        if c:
                            for r, o in pair:
                                ins = M(o, state[:, r * PD:(r + 1) * PD], ecs[:, r * P:(r + 1) * P], start=False,
                                        stop=True, skip_group_check=True)
                    ins.then_inc(y_done, 1)
                    if c < NCH - 1:
                        pe.wait_ge(bst_ready, k * 2 + 2)
                        pe.wait_ge(x_ready, k * 2 + 2)
                        pe.wait_ge(state_ready, g * 3 + (c + 1))
                        M(p_st[:, :], bt_st, xw, start=True, stop=True).then_inc(states_done, 1)
            def mix(n, i, tu):
                pe.wait_ge(mixin_ready, i * 4 + (2 * n + 2))
                pe.wait_ge(evacuated, lin(tu, 1, 1))
                for c in range(NCH):
                    cols = slice(c * P, (c + 1) * P)
                    ins = M(p_y[:, cols], vst[n][:, cols], sguw[n][:, 0:P], start=True, stop=True)
                ins.then_inc(mix_done, 1)

            with pe.Fori(0, KT // 2 - 1) as i:
                for n in range(2):
                    tu, tg = (T_UG + 2 * n, 4, i), (T_UG + 2 * n + 1, 4, i)
                    project(at(tu, 1))
                    project(at(tg, 1))
                    mix(n, i, tu)
            for n in range(2):
                tu = (T_OB - 4 + 2 * n, 0, None)
                project(at(tu, 1))
                if n == 0:
                    project(at(tu, 2))
                mix(n, KT // 2 - 1, tu)
            project((T_OB, 0, None), 1)
            pe.wait_ge(ysq_added, KT + 2)
            sum_squares()
            with pe.Fori(0, KT // 2 - 1) as i:
                for j in range(2):
                    project((T_OB + 1 + j, 2, i))
            project((T_OA - 1, 0, None))
            project((T_OA, 0, None), 2)
            with pe.Fori(0, KT // 2 - 1) as i:
                for j in range(2):
                    project((T_OA + 1 + j, 2, i))
            project((T_AT - 1, 0, None))
            project((T_AT, 0, None), 3)
            pe.wait_ge(hsq_added, KT)
            sum_squares()

            def scores(j, h1):
                zb = p_s1 if j == 1 else p_s0
                pe.wait_ge(evacuated, h1 * 4 + (T_AT + 4))
                pe.wait_ge(e_ready, h1 * 3 + (2 if j == 2 else 1))
                at_col = 0
                for b in ((0, 1), (2,), (3,))[j]:
                    n = (b + 1) * P
                    ins = M(zb[:, at_col:at_col + n], q_t[:, b * P:n], k_t[:, 0:n], start=True, stop=True)
                    at_col += n
                ins.then_inc(z_done, 1)

            def turn_weights(j, h1):
                pe.wait_ge(w_soft, h1 * 3 + (j + 1))
                pe.wait_ge(wtr_copied, h1 * 3 + (j + 1))
                for b in range(4 if j == 2 else 3):
                    ins = nc.tensor.transpose(p_tr[:, b * P:(b + 1) * P], sc_t[:, b * P:(b + 1) * P], ident)
                ins.then_inc(wtr_done, 1)

            def attend_values(h1):
                pe.wait_ge(v_taken, h1 + 1)
                pe.wait_ge(wtr_copied, h1 * 3 + 4)
                pe.wait_ge(yo_ready, h1 + 1)
                for j in range(NCH):
                    ins = M(p_y[:, j * P:T], v_cur[:, j * P:(j + 1) * P], w_t[:, j, j * P:T], start=(j == 0), stop=(j == NCH - 1))
                ins.then_inc(pv_done, 1)

            def head(t, h, attend, ahead=4):
                for j in range(4):
                    if attend and j < 3:
                        scores(j, h - 1)
                    if j < ahead:
                        project(at(t, j + 1))
                    if attend:
                        turn_weights(j, h - 1) if j < 3 else attend_values(h - 1)
                    if j == 0:
                        pe.wait_ge(evacuated, lin(t, 1, 1))
                        if attend:
                            pe.wait_ge(vtr_copied, h)
                        for c in range(NCH):
                            ins = nc.tensor.transpose(p_tv[:, c * P:(c + 1) * P], v_t[:, c * P:(c + 1) * P], ident)
                        ins.then_inc(vtr_done, 1)

            head((T_AT, 0, None), 0, False)
            with pe.Fori(1, HEADS_C - 1) as h:
                head((T_AT, 4, h), h, True)
            last = HEADS_C - 1
            head((T_AT + 4 * last, 0, None), last, True, 3)
            t0, t1, t2 = ((T_OO + f, 0, None) for f in range(3))

            def part_of(t, first, end, first_of):
                pe.wait_ge(w_ready, lin(t, 2, 1 + first // HK))
                for k in range(first, end):
                    ins = products(t, k, first_of)
                return ins

            pe.wait_ge(evacuated, T_OO - 1)
            part_of(t0, 0, HK, 4).then_inc(w_used, 1)
            scores(0, last)
            part_of(t0, HK, last, 4)
            turn_weights(0, last)
            scores(1, last)
            part_of(t1, 0, HK, None)
            turn_weights(1, last)
            scores(2, last)
            part_of(t1, HK, last, None)
            pe.wait_ge(vtr_copied, HEADS_C)
            part_of(t2, 0, 2, None)
            turn_weights(2, last)
            part_of(t2, 2, 4, None)
            attend_values(last)
            part_of(t2, 4, HK, None)
            products(t0, last, 4).then_inc(w_used, 1)
            products(t1, last, None, w_used).then_inc(w_used, 1)
            pe.wait_ge(w_ready, lin(t2, 2, 2))
            products(t2, HK, None, w_used)
            part_of(t2, HK + 1, KT, None).then_inc(w_used, 1)
            for f in range(3, KT):
                project((T_OO + f, 0, None))
            pe.wait_ge(hsq_added, 2 * KT - 1)
            for dst, src in ((p_st, ssum), (p_tv, sq2[(KT - 1) % 2])):
                for c in range(NCH):
                    ins = M(dst[:, c:c + 1], src[:, c * P:(c + 1) * P], ones[:, 0:1], start=True, stop=True)
                ins.then_inc(fsum_done, 1)
                if src is ssum:
                    pe.wait_ge(hsq_ready, 2 * KT)
            pe.wait_ge(frstd_ready, 1)
            for dst in (p_y, p_s0):
                for c in range(NCH):
                    ins = M(dst[:, c * P:(c + 1) * P], frstd[:, c:c + 1].to_broadcast([P, P]), ident, start=True, stop=True)
                ins.then_inc(spread_done, 1)


def _tiles(w):
    n = w.shape[1] // P
    return w.reshape(2, HK, P, n, P).transpose(3, 0, 2, 1, 4).reshape(2 * n, P, HK * P)


def _per_feature(v):
    return v.reshape(-1, P).T


def kernel(**inputs):
    import concourse.bacc as bacc
    from concourse.bass_utils import run_bass_kernel_spmd

    a = {k: np.asarray(v) for k, v in inputs.items()}
    f32 = np.float32
    w_in = a["ev_w_in"][0]
    z, x, b, c, dt, g, u, v = np.split(w_in, np.cumsum([D, D, 512, 512, HEADS_A, D, D]), axis=1)
    ug = np.stack([u.reshape(D, KT, P), g.reshape(D, KT, P)], axis=2).reshape(D, 2 * D)
    padded = np.concatenate([dt, np.zeros((D, P - HEADS_A), f32)], axis=1)
    w_out = a["ev_w_out"][0]
    q, k, vv, gg = (m.reshape(D, KT, P) for m in np.split(a["od_w_in"][0], 4, axis=1))
    heads = np.stack([vv, gg, q, k], axis=2).reshape(D, 4 * D)
    weights = np.concatenate([_tiles(m) for m in (padded, b, c, x, z, v, ug, w_out[D:], w_out[:D], heads,
                                                  a["od_w_out"][0])])
    order = np.concatenate([np.arange(D, D + 1024), np.arange(D)])
    cw = a["ev_conv_w"][0][:, order].reshape(4, NCONV, P).transpose(2, 1, 0).reshape(P, 4 * NCONV)
    table = np.zeros((P, C_END), f32)
    table[:, C_NW0:C_NW1] = _per_feature(a["norm_w"][0])
    table[:, C_NW1:C_FNW] = _per_feature(a["norm_w"][1])
    table[:, C_FNW:C_SSDW] = _per_feature(a["final_norm_w"])
    table[:, C_SSDW:C_CW] = _per_feature(a["ev_ssd_norm_w"][0])
    table[:, C_CW:C_CB] = cw
    table[:, C_CB:C_D] = _per_feature(a["ev_conv_b"][0][order])
    table[:, C_D:C_DTB] = a["ev_d_skip"][0][None, :]
    table[:HEADS_A, C_DTB] = a["ev_dt_bias"][0]
    table[:HEADS_A, C_ALOG] = a["ev_a_log"][0]
    r, s = np.arange(P)[:, None], np.arange(P)[None, :]
    shapes = np.concatenate([(r == s), np.ones((P, P)), (r <= s), (s < r), np.where(s < r, 0.0, -1e30)], axis=1).astype(f32)
    arrays = {
        "xT": np.ascontiguousarray(a["x"][0].T).reshape(KT, P, T),
        "weights": weights,
        "table": table,
        "shapes": shapes,
        "sgu_wT": np.ascontiguousarray(a["ev_sgu_w"][0].transpose(0, 2, 1)),
        "sgu_rows": np.concatenate([a["ev_sgu_ln_w"][0].reshape(KT, P), a["ev_sgu_ln_b"][0].reshape(KT, P), a["ev_sgu_b"][0]], axis=1),
    }
    nc = bacc.Bacc("TRN2", target_bir_lowering=False, num_devices=1)
    args = {n: nc.dram_tensor(n, m.shape, mybir.dt.float32, kind="ExternalInput").ap() for n, m in arrays.items()}
    out = nc.dram_tensor("out", (KT, P, T), mybir.dt.float32, kind="ExternalOutput").ap()
    trunk(nc, **args, out=out)
    got = run_bass_kernel_spmd(nc, [arrays], core_ids=[0]).results[0]["out"]
    return np.ascontiguousarray(got.reshape(D, T).T)[None]
```
